# Optimizing a Trainium2 kernel written in Bass

```python
import jax, jax.numpy as jnp
from jax import lax
import numpy as np

D_MODEL = 1024
BATCH = 1
SEQ = 512
DEPTH = 1

N_META = 16
EPS = 1e-6
NEG = -1e30
M_HEADS = 8
M_DQK = 64
M_DV = 128
M_CHUNK = 64
A_HEADS = 8
A_NOPE = 128
A_ROPE = 64
A_DV = 128
Q_LORA = 256
KV_LORA = 128
ROPE_THETA = 10000.0
Q_BLOCK = 128
N_EXPERTS = 32
TOP_K = 4
D_FF = 1024
SWIGLU_ALPHA = 1.702
SWIGLU_LIMIT = 7.0
MOE_BLOCK = 128
IN_SIZES = (M_HEADS * M_DQK, M_HEADS * M_DQK, M_HEADS * M_DV, M_HEADS * M_DV,
            2 * M_HEADS, 2 * M_HEADS, Q_LORA, KV_LORA, A_ROPE, 2 * D_MODEL)
D_IN = sum(IN_SIZES)
IN_OFFSETS = tuple(int(s) for s in np.cumsum(IN_SIZES)[:-1])

kernel_name = 'hybrid_mlstm_mla_moe_encoder'

def rms_norm(x, g):
    xf = x.astype(jnp.float32)
    y = xf * lax.rsqrt(jnp.mean(xf * xf, axis=-1, keepdims=True) + EPS)
    return (y * g.astype(jnp.float32)).astype(x.dtype)

def rope(x, pos):
    half = x.shape[-1] // 2
    freqs = ROPE_THETA ** (-jnp.arange(half, dtype=jnp.float32) / half)
    ang = pos.astype(jnp.float32)[:, None] * freqs[None, :]
    cos, sin = jnp.cos(ang).astype(x.dtype), jnp.sin(ang).astype(x.dtype)
    x1, x2 = x[..., :half], x[..., half:]
    return jnp.concatenate([x1 * cos - x2 * sin, x1 * sin + x2 * cos], axis=-1)

def mlstm_scan(q, k, v, li, lf):
    B, H, Lp, _ = q.shape
    nc = Lp // M_CHUNK

    def chunks(a):
        a = a.reshape(B, H, nc, M_CHUNK, *a.shape[3:])
        return jnp.moveaxis(a, 2, 0)

    tril = jnp.tril(jnp.ones((M_CHUNK, M_CHUNK), dtype=bool))

    def step(carry, inp):
        C, n, m = carry
        qc, kc, vc, lic, lfc = inp
        b = jnp.cumsum(lfc, axis=-1)
        dmat = jnp.where(tril, b[..., :, None] - b[..., None, :] + lic[..., None, :], NEG)
        m_inter = b + m[..., None]
        m_t = jnp.maximum(m_inter, dmat.max(axis=-1))
        w = jnp.exp(dmat - m_t[..., None]) * jnp.einsum('bhtd,bhsd->bhts', qc, kc)
        s_inter = jnp.exp(m_inter - m_t)
        num = s_inter[..., None] * jnp.einsum('bhtd,bhdv->bhtv', qc, C) + jnp.einsum('bhts,bhsv->bhtv', w, vc)
        den = s_inter * jnp.einsum('bhtd,bhd->bht', qc, n) + w.sum(axis=-1)
        h = num / jnp.maximum(jnp.abs(den), jnp.exp(-m_t))[..., None]
        b_last = b[..., -1]
        g = b_last[..., None] - b + lic
        m_new = jnp.maximum(b_last + m, g.max(axis=-1))
        decay = jnp.exp(b_last + m - m_new)
        wk = jnp.exp(g - m_new[..., None])
        C_new = decay[..., None, None] * C + jnp.einsum('bhs,bhsd,bhsv->bhdv', wk, kc, vc)
        n_new = decay[..., None] * n + jnp.einsum('bhs,bhsd->bhd', wk, kc)
        return (C_new, n_new, m_new), h

    init = (jnp.zeros((B, H, q.shape[-1], v.shape[-1]), jnp.float32),
            jnp.zeros((B, H, q.shape[-1]), jnp.float32),
            jnp.zeros((B, H), jnp.float32))
    _, hs = lax.scan(step, init, (chunks(q), chunks(k), chunks(v), chunks(li), chunks(lf)))
    return jnp.moveaxis(hs, 0, 2).reshape(B, H, Lp, v.shape[-1])

def mlstm_branch(q, k, v, o_pre, i_pre, f_pre, b_i, b_f, g_norm):
    B, L, _ = q.shape
    pad = M_CHUNK - N_META
    Lp = L + pad

    def heads(a, d):
        a = a.astype(jnp.float32).reshape(B, L, M_HEADS, d)
        a = jnp.pad(a, ((0, 0), (pad, 0), (0, 0), (0, 0)))
        return a.transpose(0, 2, 1, 3)

    qh = heads(q, M_DQK) * (M_DQK ** -0.5)
    kh = heads(k, M_DQK)
    vh = heads(v, M_DV)
    valid = (jnp.arange(Lp) >= pad)[None, :, None, None]
    i_all = jnp.pad(i_pre.astype(jnp.float32).reshape(B, L, 2, M_HEADS) + b_i.astype(jnp.float32),
                    ((0, 0), (pad, 0), (0, 0), (0, 0)))
    f_all = jnp.pad(f_pre.astype(jnp.float32).reshape(B, L, 2, M_HEADS) + b_f.astype(jnp.float32),
                    ((0, 0), (pad, 0), (0, 0), (0, 0)))
    li = jnp.where(valid, i_all, NEG).transpose(0, 2, 3, 1)
    lf = jnp.where(valid, jax.nn.log_sigmoid(f_all), 0.0).transpose(0, 2, 3, 1)
    flip = lambda a: jnp.flip(a, axis=2)
    h_fwd = mlstm_scan(qh, kh, vh, li[:, 0], lf[:, 0])
    h_bwd = flip(mlstm_scan(flip(qh), flip(kh), flip(vh), flip(li[:, 1]), flip(lf[:, 1])))
    h = (h_fwd + h_bwd)[:, :, pad:]
    h = rms_norm(h, g_norm[:, None, :])
    h = h.transpose(0, 2, 1, 3).reshape(B, L, M_HEADS * M_DV).astype(q.dtype)
    return h * jax.nn.sigmoid(o_pre.astype(jnp.float32)).astype(q.dtype)

def mla_branch(cq, ckv, k_rope, w_uq, w_ukv, g_q, g_kv, pos):
    B, L, _ = cq.shape
    q = jnp.einsum('blr,rhd->bhld', rms_norm(cq, g_q), w_uq)
    q_nope, q_rope = q[..., :A_NOPE], rope(q[..., A_NOPE:], pos)
    kv = jnp.einsum('blr,rhd->bhld', rms_norm(ckv, g_kv), w_ukv)
    k_nope, v = kv[..., :A_NOPE], kv[..., A_NOPE:]
    k_r = rope(k_rope, pos)
    scale = (A_NOPE + A_ROPE) ** -0.5

    def attend(qn, qr):
        s = jnp.einsum('bhqd,bhkd->bhqk', qn, k_nope) + jnp.einsum('bhqd,bkd->bhqk', qr, k_r)
        p = jax.nn.softmax(s.astype(jnp.float32) * scale, axis=-1).astype(v.dtype)
        return jnp.einsum('bhqk,bhkd->bhqd', p, v)

    out_meta = attend(q_nope[:, :, :N_META], q_rope[:, :, :N_META])
    nb = (L - N_META) // Q_BLOCK

    def blocks(a):
        a = a[:, :, N_META:].reshape(B, A_HEADS, nb, Q_BLOCK, a.shape[-1])
        return jnp.moveaxis(a, 2, 0)

    out_real = lax.map(lambda qs: attend(qs[0], qs[1]), (blocks(q_nope), blocks(q_rope)))
    out_real = jnp.moveaxis(out_real, 0, 2).reshape(B, A_HEADS, L - N_META, A_DV)
    out = jnp.concatenate([out_meta, out_real], axis=2)
    return out.transpose(0, 2, 1, 3).reshape(B, L, A_HEADS * A_DV)

def moe(x, w_router, b_router, w1, b1, w2, b2):
    B, L, D = x.shape
    xt = x.reshape(-1, D)
    T = xt.shape[0]
    logits = (xt @ w_router).astype(jnp.float32) + b_router.astype(jnp.float32)
    top_val, top_idx = lax.top_k(logits, TOP_K)
    gates = jax.nn.softmax(top_val, axis=-1)
    n = T * TOP_K
    flat_e = top_idx.reshape(-1)
    flat_tok = jnp.repeat(jnp.arange(T, dtype=jnp.int32), TOP_K)
    flat_w = gates.reshape(-1)
    order = jnp.argsort(flat_e)
    sorted_e = flat_e[order]
    counts = jnp.bincount(flat_e, length=N_EXPERTS)
    start = jnp.cumsum(counts) - counts
    padded = (counts + MOE_BLOCK - 1) // MOE_BLOCK * MOE_BLOCK
    padded_end = jnp.cumsum(padded)
    padded_start = padded_end - padded
    dest = padded_start[sorted_e] + jnp.arange(n, dtype=jnp.int32) - start[sorted_e]
    nb = -(-n // MOE_BLOCK) + N_EXPERTS
    buf_tok = jnp.full((nb * MOE_BLOCK,), T, jnp.int32).at[dest].set(flat_tok[order])
    buf_w = jnp.zeros((nb * MOE_BLOCK,), jnp.float32).at[dest].set(flat_w[order])
    block_e = jnp.minimum(jnp.searchsorted(padded_end, jnp.arange(nb, dtype=jnp.int32) * MOE_BLOCK, side='right'),
                          N_EXPERTS - 1)
    x_pad = jnp.concatenate([xt, jnp.zeros((1, D), xt.dtype)], axis=0)

    def expert_block(args):
        toks, wts, e = args
        hid = x_pad[toks] @ w1[e] + b1[e]
        glu = jnp.minimum(hid[..., :D_FF], SWIGLU_LIMIT)
        lin = jnp.clip(hid[..., D_FF:], -SWIGLU_LIMIT, SWIGLU_LIMIT)
        act = glu * jax.nn.sigmoid(SWIGLU_ALPHA * glu) * (lin + 1)
        return (act @ w2[e] + b2[e]).astype(jnp.float32) * wts[:, None]

    yb = lax.map(expert_block, (buf_tok.reshape(nb, MOE_BLOCK), buf_w.reshape(nb, MOE_BLOCK), block_e))
    y = jnp.zeros((T + 1, D), jnp.float32).at[buf_tok].add(yb.reshape(-1, D))[:T]
    return y.astype(x.dtype).reshape(B, L, D)

def setup_inputs(seed: int = 0) -> dict:
    key = jax.random.key(seed)
    ks = jax.random.split(key, 22)
    f32 = jnp.float32

    def nrm(k, shape, scale):
        return jax.random.normal(k, shape, f32) * scale

    def gain(k, shape):
        return 1.0 + 0.02 * jax.random.normal(k, shape, f32)

    f_bias = jnp.linspace(3.0, 6.0, M_HEADS, dtype=f32)[None, None, :]
    return {
        'x': nrm(ks[0], (BATCH, SEQ, D_MODEL), 1.0),
        'meta_tokens': nrm(ks[1], (N_META, D_MODEL), 1.0),
        'norm_mix': gain(ks[2], (DEPTH, D_MODEL)),
        'w_in': nrm(ks[3], (DEPTH, D_MODEL, D_IN), D_MODEL ** -0.5),
        'm_b_i': nrm(ks[4], (DEPTH, 2, M_HEADS), 0.1),
        'm_b_f': f_bias + nrm(ks[5], (DEPTH, 2, M_HEADS), 0.1),
        'm_norm': gain(ks[6], (DEPTH, M_HEADS, M_DV)),
        'w_m_proj': nrm(ks[7], (DEPTH, M_HEADS * M_DV, D_MODEL), (M_HEADS * M_DV) ** -0.5),
        'a_w_uq': nrm(ks[8], (DEPTH, Q_LORA, A_HEADS, A_NOPE + A_ROPE), Q_LORA ** -0.5),
        'a_w_ukv': nrm(ks[9], (DEPTH, KV_LORA, A_HEADS, A_NOPE + A_DV), KV_LORA ** -0.5),
        'a_norm_q': gain(ks[10], (DEPTH, Q_LORA)),
        'a_norm_kv': gain(ks[11], (DEPTH, KV_LORA)),
        'w_a_proj': nrm(ks[12], (DEPTH, A_HEADS * A_DV, D_MODEL), (A_HEADS * A_DV) ** -0.5),
        'w_out': nrm(ks[13], (DEPTH, D_MODEL, D_MODEL), D_MODEL ** -0.5),
        'norm_ffn': gain(ks[14], (DEPTH, D_MODEL)),
        'w_router': nrm(ks[15], (DEPTH, D_MODEL, N_EXPERTS), D_MODEL ** -0.5),
        'b_router': nrm(ks[16], (DEPTH, N_EXPERTS), 0.01),
        'w1': nrm(ks[17], (DEPTH, N_EXPERTS, D_MODEL, 2 * D_FF), D_MODEL ** -0.5),
        'b1': nrm(ks[18], (DEPTH, N_EXPERTS, 2 * D_FF), 0.01),
        'w2': nrm(ks[19], (DEPTH, N_EXPERTS, D_FF, D_MODEL), D_FF ** -0.5),
        'b2': nrm(ks[20], (DEPTH, N_EXPERTS, D_MODEL), 0.01),
        'norm_final': gain(ks[21], (D_MODEL,)),
    }

def reference(x, meta_tokens, norm_mix, w_in, m_b_i, m_b_f, m_norm, w_m_proj,
              a_w_uq, a_w_ukv, a_norm_q, a_norm_kv, w_a_proj, w_out,
              norm_ffn, w_router, b_router, w1, b1, w2, b2, norm_final):
    B = x.shape[0]
    meta = jnp.broadcast_to(meta_tokens.astype(x.dtype)[None], (B, N_META, D_MODEL))
    h = jnp.concatenate([meta, x], axis=1)
    pos = jnp.arange(h.shape[1], dtype=jnp.int32)
    for l in range(DEPTH):
        u = rms_norm(h, norm_mix[l])
        z = u @ w_in[l]
        m_q, m_k, m_v, m_o, m_i, m_f, a_cq, a_ckv, a_kr, gate_pre = jnp.split(z, list(IN_OFFSETS), axis=-1)
        y_m = mlstm_branch(m_q, m_k, m_v, m_o, m_i, m_f, m_b_i[l], m_b_f[l], m_norm[l]) @ w_m_proj[l]
        y_a = mla_branch(a_cq, a_ckv, a_kr, a_w_uq[l], a_w_ukv[l], a_norm_q[l], a_norm_kv[l], pos) @ w_a_proj[l]
        gates = jax.nn.sigmoid(gate_pre.astype(jnp.float32)).astype(h.dtype)
        mixed = gates[..., :D_MODEL] * y_m + gates[..., D_MODEL:] * y_a
        h = h + mixed @ w_out[l]
        h = h + moe(rms_norm(h, norm_ffn[l]), w_router[l], b_router[l], w1[l], b1[l], w2[l], b2[l])
    return rms_norm(h, norm_final)[:, N_META:]


_drawn_inputs = setup_inputs


def setup_inputs(seed=0):
    import zlib

    import numpy as np

    out = dict(_drawn_inputs(seed))
    spreads = {}
    factors = {'m_b_i': 22.425,
     'a_norm_q': 5.521,
     'a_norm_kv': 4.253,
     'b1': 21.918,
     'b2': 25.136,
     'norm_final': 7.527,
     'm_norm': 6.429,
     'norm_ffn': 2.782,
     'b_router': 3.472}
    for name, (base, spread) in spreads.items():
        noise = np.random.default_rng([zlib.crc32(name.encode()), seed]).standard_normal(out[name].shape)
        drawn = base * np.exp(spread * noise) if base else spread * noise
        out[name] = __import__('jax').numpy.asarray(drawn.astype(out[name].dtype))
    for name, factor in factors.items():
        out[name] = (out[name] * factor).astype(out[name].dtype)
    return out
```

```python
import numpy as np
from contextlib import ExitStack

import concourse.bass as bass
from concourse import mybir

F32 = mybir.dt.float32
BF16 = mybir.dt.bfloat16
I32 = mybir.dt.int32
ALU = mybir.AluOpType
ACT = mybir.ActivationFunctionType
AX = mybir.AxisListType

P = 128
D = 1024
KT = D // P
T = 512
META = 16
MT = T // P
TK = T + META
H = 8
PAIRS = H // 2
DQK, DV = 64, 128
NOPE, ROPE, ADV = 128, 64, 128
QL, KVL = 256, 128
E = 32
TOPK = 4
FF = 1024
BANK = 512
SLOT = 2048
SLOTS = 12
NEG = -1e30
EPS = 1e-6
C_Q, C_K, C_V, C_O = 0, 512, 1024, 2048
C_IF, C_CQ, C_CKV, C_KR, C_G = 3072, 3104, 3360, 3488, 3552
C_MISC = C_G - C_IF
MAXOVER = T * TOPK // P - 1
BLOCKS = E + 16

ACT_ML, DVE_ML, DVE_AT, DVE_MX = 24, 41, 21, 2

K_ID, K_ONE, K_MF, K_MB, K_US, K_IO, K_EPS, K_HALF, K_END = 0, 128, 256, 384, 512, 640, 672, 673, 674


def constant_tables():
    c = np.zeros((P, K_END), np.float32)
    s, t = np.arange(P)[:, None], np.arange(P)[None, :]
    c[:, K_ID:K_ID + P] = s == t
    c[:, K_ONE:K_ONE + P] = 1
    c[:, K_MF:K_MF + P] = np.where(s <= t, 0.0, NEG)
    c[:, K_MB:K_MB + P] = np.where(s >= t, 0.0, NEG)
    c[:, K_US:K_US + P] = s < t
    c[:, K_IO:K_IO + E] = np.arange(E)
    c[:, K_EPS] = EPS
    c[:, K_HALF] = -0.5
    half = ROPE // 2
    freqs = np.float32(10000.0) ** (-np.arange(half, dtype=np.float32) / np.float32(half))
    pos = np.concatenate([np.arange(META, TK), np.arange(META)]).astype(np.float32)
    ang = (pos[None, :] * freqs.astype(np.float32)[:, None]).astype(np.float32)
    cos, sin = np.cos(ang).astype(np.float32), np.sin(ang).astype(np.float32)
    rope = np.stack([np.tile(cos, (4, 1)), np.concatenate([-sin, sin, -sin, sin])], 1)
    tok = (np.arange(P)[:, None] + P * np.arange(MT)[None, :]).astype(np.int32)
    return {"c_table": c, "c_rope": np.ascontiguousarray(rope), "c_tok": tok,
            "c_zero": np.zeros((P, BLOCKS), np.int32)}


class Steps:

    def __init__(self, eng, sem, start=0, per=None):
        self.eng, self.sem, self.start, self.per, self.n = eng, sem, start, per, 0

    def did(self, ins):
        ins.then_inc(self.sem, 1)
        self.n += 1

    def settle(self):
        self.eng.wait_ge(self.sem, self.start + self.n)

    def alone(self, ins):
        self.did(ins)
        self.settle()

    def end(self):
        assert self.per is None or self.per == self.n, (self.per, self.n)
        return self.n


def program(nc, x, meta, norm_mix, w_in, m_b_i, m_b_f, m_norm, w_m_proj, w_uq, w_ukv, a_norm_q,
            a_norm_kv, w_a_proj, w_out, norm_ffn, w_router, b_router, w1, b1, w2, b2, norm_final,
            c_table, c_rope, c_tok, c_zero, out):
    with ExitStack() as ctx:
        build(ctx, nc, x, meta, norm_mix, w_in, m_b_i, m_b_f, m_norm, w_m_proj, w_uq, w_ukv,
              a_norm_q, a_norm_kv, w_a_proj, w_out, norm_ffn, w_router, b_router, w1, b1, w2, b2,
              norm_final, c_table, c_rope, c_tok, c_zero, out)


def build(ctx, nc, x, meta, norm_mix, w_in, m_b_i, m_b_f, m_norm, w_m_proj, w_uq, w_ukv, a_norm_q,
          a_norm_kv, w_a_proj, w_out, norm_ffn, w_router, b_router, w1, b1, w2, b2, norm_final,
          c_table, c_rope, c_tok, c_zero, out):
    def sb(name, cols, dt=F32, rows=P):
        return ctx.enter_context(nc.sbuf_tensor(name, [rows, cols], dt))

    def sem(name):
        return ctx.enter_context(nc.semaphore(name))

    def dram(name, shape, dt):
        return nc.dram_tensor(name, shape, dt, kind="Internal").ap()

    def view(t, at, *dims):
        n = 1
        for d in dims:
            n *= d
        v = t[:, at:at + n]
        if len(dims) == 2:
            v = v.rearrange("p (a b) -> p a b", a=dims[0])
        elif len(dims) == 3:
            v = v.rearrange("p (a b c) -> p a b c", a=dims[0], b=dims[1])
        return v

    ct = sb("ct", K_END)
    ident, ones = ct[:, K_ID:K_ID + P], ct[:, K_ONE:K_ONE + P]
    mask_f, mask_b = ct[:, K_MF:K_MF + P], ct[:, K_MB:K_MB + P]
    before = ct[:, K_US:K_US + P]
    expert_no = ct[:, K_IO:K_IO + E]
    eps_col, half_col = ct[:, K_EPS:K_EPS + 1], ct[:, K_HALF:K_HALF + 1]
    x_sb = sb("x_sb", MT * D)
    xs = view(x_sb, 0, MT, D)
    ring = sb("ring", SLOTS * SLOT)
    uT_sb = sb("uT_sb", KT * TK)
    uT = view(uT_sb, 0, KT, TK)
    hm_sb = sb("hm_sb", H * T)
    hmT = view(hm_sb, 0, H, T)
    at_sb = sb("at_sb", H * T)
    attT = view(at_sb, 0, H, T)
    mix_sb = sb("mix_sb", KT * T)
    mixT = view(mix_sb, 0, KT, T)
    low_sb = sb("low_sb", 2 * T + 2 * TK)
    cqT = view(low_sb, 0, 2, T)
    ckvT = view(low_sb, 2 * T, TK)
    krT = view(low_sb, 2 * T + TK, TK)
    small = sb("small", 1800)
    at_small = [0]

    def col(*dims):
        n = 1
        for d in dims:
            n *= d
        at_small[0] += n
        assert at_small[0] <= 1800, at_small
        return view(small, at_small[0] - n, *dims)

    g_mix = col(KT)
    g_q, g_kv = col(2), col(1)
    g_m = col(H)
    gate_bias = col(1)
    ss, rstd = col(8), col(8)
    a_col = col(MT + 1, 64)
    em_col = col(MT, 64)
    a_pair = col(MT + 1, 2, 2)
    em_pair = col(MT, 2, 2)
    g_pair = col(2)
    den = col(2, MT, 2)
    rden = col(2, MT, 2)
    hss, hrs = col(2, MT), col(2, MT)
    neg_max, row_sum, row_inv = col(8), col(8), col(8)

    PS = ctx.enter_context(nc.psum_tensor("PS", [P, 8, BANK], F32))

    m_dram = dram("m_dram", [64, T], F32)

    dve_steps, act_steps, pool_steps = sem("dve_steps"), sem("act_steps"), sem("pool_steps")
    const_in, small_in, misc_in, rope_in = map(sem, ("const_in", "small_in", "misc_in", "rope_in"))
    x_tile_in = [sem(f"x_tile_in{m}") for m in range(MT + 1)]
    pe_ut, un_ready, rstd_ready, ut_ready = map(sem, ("pe_ut", "un_ready", "rstd_ready", "ut_ready"))
    sumsq_x = sem("sumsq_x")
    pad_ready, ones_ready = sem("pad_ready"), sem("ones_ready")
    half_bc = half_col.broadcast_to([P, MT])
    junk2 = view(at_sb, 0, T)
    pe_if, pe_cq, pe_ckv, pe_kr, pe_sum, pe_gt = map(sem, ("pe_if", "pe_cq", "pe_ckv", "pe_kr", "pe_sum", "pe_gt"))
    sq_ready, root_ready, if_used, gates_ready, low_used = map(sem, ("sq_ready", "root_ready", "if_used", "gates_ready", "low_used"))
    minus_abs, soft_ready, m_ready, em_rows, m_stored = map(sem, ("minus_abs", "soft_ready", "m_ready", "em_rows", "m_stored"))
    misc_done = sem("misc_done")
    ml_w = [sem(f"ml_w{n}") for n in range(3)]
    ml_m = sem("ml_m")
    pe_q, pe_k, pe_v, pe_s, pe_o, pe_pv, pe_t = map(sem, ("pe_q", "pe_k", "pe_v", "pe_s", "pe_o", "pe_pv", "pe_t"))
    diag_ready, decay_ready, q_ready, k_ready, v_ready, s_used, oexp_ready, o_used = map(
        sem, ("diag_ready", "decay_ready", "q_ready", "k_ready", "v_ready", "s_used", "oexp_ready", "o_used"))
    pv_used, hss_ready, hrs_ready, h_ready, t_used = map(sem, ("pv_used", "hss_ready", "hrs_ready", "h_ready", "t_used"))
    at_w = sem("at_w")
    swap_ready, pe_aq, pe_ak, pe_av, pe_av2 = map(sem, ("swap_ready", "pe_aq", "pe_ak", "pe_av", "pe_av2"))
    aq_ready, ar_ready, ak_ready, av_ready = map(sem, ("aq_ready", "ar_ready", "ak_ready", "av_ready"))
    pe_sc, max_ready, exp_ready, p_ready, pe_pt, ptx_ready, ptm_ready, pe_ao, ao_ready = map(
        sem, ("pe_sc", "max_ready", "exp_ready", "p_ready", "pe_pt", "ptx_ready", "ptm_ready", "pe_ao", "ao_ready"))
    gx_w = [sem(f"gx_w{n}") for n in range(4)]
    pe_g, sig_ready, mix_ready = map(sem, ("pe_g", "sig_ready", "mix_ready"))
    wo_in, pe_h, h_out = map(sem, ("wo_in", "pe_h", "h_out"))

    w_r_sb = sb("w_r_sb", KT * E)
    b1_row = sb("b1_row", 2 * FF, BF16, 3)
    b1_part = sb("b1_part", 2 * FF, BF16, E)
    ones3 = sb("ones3", P, BF16, 3)
    ints = sb("ints", 104, I32)
    drow_i, yrow_i, over_i = ints[:, 0:16], ints[:, 16:32], ints[:, 32:49]
    drow_by = drow_i.rearrange("p (m k) -> p m k", m=MT)
    disp, tok_i, idx_now = ints[:, 50:50 + BLOCKS], ints[:, 98:98 + MT], ints[:, 102:103]
    b_r, top8, n_gt, cnt, n_over, cum_over, shift = col(E), col(MT, 8), col(MT), col(E), col(E), col(E), col(E)
    ov_f, drow_f, yrow_f, gate_k = col(16), col(MT, TOPK), col(MT, TOPK), col(MT, TOPK)
    gT = view(uT_sb, 0, T)
    zeros = view(at_sb, 2 * D, D)
    waits_passed = sem("waits_passed")
    zeros_ready, y_zeroed = sem("zeros_ready"), sem("y_zeroed")
    gains_in, wr_in, b1f_in, b1_stored, xh_ready, xh_rstd, xt_ready, xt_stored, pe_xt, xtT_ready, pe_lg = map(sem, (
        "gains_in", "wr_in", "b1f_in", "b1_stored", "xh_ready", "xh_rstd", "xt_ready", "xt_stored", "pe_xt", "xtT_ready", "pe_lg"))
    ex_in, ex_ready, sel_ready, pe_pos, rows_ready, table_ready, zero_in, placed, disp_in = map(sem, (
        "ex_in", "ex_ready", "sel_ready", "pe_pos", "rows_ready", "table_ready", "zero_in", "placed", "disp_in"))
    g_all_ready, pe_gT, gT_ready, pe_b2, b2_added = map(sem, ("g_all_ready", "pe_gT", "gT_ready", "pe_b2", "b2_added"))
    chunk_in = [sem(f"chunk_in{c}") for c in range(SLOTS)]
    b1_in, idx_ready, xg_in, pe_tx, xgT_ready, half_used, pe_hid, hid_used = map(sem, (
        "b1_in", "idx_ready", "xg_in", "pe_tx", "xgT_ready", "half_used", "pe_hid", "hid_used"))
    down_used, h_sum = sem("down_used"), sem("h_sum")
    g_ready, s_ready, act_ready, pe_ta, actT_ready, pe_y, y_ready, y_out = map(sem, (
        "g_ready", "s_ready", "act_ready", "pe_ta", "actT_ready", "pe_y", "y_ready", "y_out"))
    expert_steps, end_steps = sem("expert_steps"), sem("end_steps")
    y_back = [sem(f"y_back{m}") for m in range(MT)]
    end_ready, end_rstd, out_ready, out_stored = map(sem, ("end_ready", "end_rstd", "out_ready", "out_stored"))

    def slot(n):
        return n * SLOT

    w_misc = view(ring, slot(0), KT, C_MISC)
    w_if = view(ring, slot(2), KT, P)
    w_kr = view(ring, slot(3), 2, KT, P)
    un = view(ring, slot(4), 2, D)
    junk = view(ring, slot(5), SLOT)
    meta_sb = view(ring, slot(6), D)
    root = view(ring, slot(7), SLOT)
    zif, g_tmp, lf_hi = (view(ring, slot(8) + n * TK, TK) for n in range(3))
    li_row, lf_row, b_row = (view(ring, slot(9) + n * TK, TK) for n in range(3))
    a_row, top_row, zero_row = (view(ring, slot(10) + n * TK, TK) for n in range(3))
    a_nat, nm_nat, em_nat = (view(ring, slot(11) + n * TK, TK) for n in range(3))
    rope = view(mix_sb, 0, 2, TK)
    cos, sin = rope[:, 0], rope[:, 1]
    wq_s, wk_s = view(ring, slot(0), KT, P), view(ring, slot(0) + KT * P, KT, P)
    wv_s, wo_s = view(ring, slot(1), KT, 2 * DV), view(ring, slot(2), KT, 2 * DV)
    DEC = 9 * T

    def dec_f(hh, j):
        return view(ring, slot(3) + hh * DEC + j * T, T)

    def dec_b(hh, j):
        return view(ring, slot(3) + hh * DEC + (5 + j) * T, T)

    def diagonal(hh, d):
        at = slot(3) + hh * DEC + d * 5 * T
        return view(ring, at, MT, T + P)[:, :, 0:P]

    m_bc = view(ring, slot(8), 2, 2, T)
    v_sb = view(ring, slot(9), MT + 1, 2, DV + 1)
    qT, kT = view(ring, slot(10), T), view(ring, slot(10) + T, TK)
    o_sb = view(ring, slot(11), 2, T)
    h_sb = view(ring, slot(11) + 2 * T, 2, MT, DV)
    w_q = view(ring, slot(0), 2, 2 * (NOPE + ROPE))
    w_swap = view(ring, slot(0) + 768, 2, 2 * ROPE)
    w_kv = view(ring, slot(0) + 1024, 2 * (NOPE + ADV))
    qn = view(ring, slot(1), 2, T)
    qr = view(ring, slot(1) + 2 * T, T)
    kn = view(ring, slot(2), 2, TK)
    va = view(ring, slot(3), MT + 1, 2 * ADV)
    pr = view(ring, slot(4), 3, TK)
    prT = view(ring, slot(5), MT + 1, T)
    r_tmp = view(ring, slot(7), 2, T)
    w_g = [view(ring, slot(9) + n * KT * P, KT, P) for n in range(4)]
    sg = view(ring, slot(11), 2, T)
    mix_tmp = view(ring, slot(11) + 2 * T, T)
    w_o = view(ring, slot(4), KT, D)

    xt_dram = dram("xt_dram", [T, D], F32)
    disp_dram = dram("disp_dram", [P * BLOCKS, 1], I32)
    y_dram = dram("y_dram", [BLOCKS * P, D], F32)
    b1_dram = dram("b1_dram", [3, E, 2 * FF], BF16)
    win = w_in.rearrange("(k p) n -> p k n", p=P)
    wuq = w_uq.rearrange("(k p) h n -> p k h n", p=P)
    wukv = w_ukv.rearrange("p h n -> p (h n)")
    wmp = w_m_proj.rearrange("(k p) n -> p k n", p=P)
    wap = w_a_proj.rearrange("(k p) n -> p k n", p=P)
    wop = w_out.rearrange("(k p) n -> p k n", p=P)

    w_r = view(w_r_sb, 0, KT, E)
    gain_f, gain_l = view(at_sb, 0, D), view(at_sb, D, D)
    xt = view(hm_sb, 0, MT, D)
    xtT = view(uT_sb, 0, KT, T)
    sq_junk = view(uT_sb, KT * T - D, D)
    rt = [view(at_sb, 2 * D + n * MT * E, MT, E) for n in range(16)]
    (lg, gt, eq, eqn, sel, ex, rank, pos, jj, blk, slot_no, yrow, drow, selk, prod, tmp_r) = rt
    ov_cmp = view(low_sb, 512, 16, E)
    b2_sb = view(low_sb, 1024, D)
    xg = view(mix_sb, 0, D)
    xgT = view(mix_sb, D, KT, P)
    act_sb = view(mix_sb, 2 * D, FF)
    actT = view(mix_sb, 3 * D, KT, P)
    y_sb = view(at_sb, 2 * D, D)
    g_sb, s_sb = view(at_sb, 3 * D, BANK), view(at_sb, 3 * D + BANK, BANK)
    l_sb = view(low_sb, 0, BANK)
    b1_f = view(low_sb, 0, 2 * FF)
    CHUNK_SLOT = [0, 1, 2, 3, 8, 9, 10, 11, 4, 5, 6, 7]
    w1_c = [view(ring, slot(CHUNK_SLOT[c]), 4, BANK) for c in range(8)]
    w2_c = [view(ring, slot(CHUNK_SLOT[8 + c]), 2, D) for c in range(4)]
    y_rows = view(ring, 0, MT * TOPK, D)
    w1v = w1.rearrange("e (k p) n -> p e k n", p=P)
    w2v = w2.rearrange("e (k p) n -> p e k n", p=P)

    def bank(b):
        return PS[:, b, :]

    def group(pe, out, pairs):
        for n, (w, r) in enumerate(pairs):
            last = nc.tensor.matmul(out, w, r, start=n == 0, stop=n == len(pairs) - 1)
        return last

    def passed(eng):
        eng.sem_inc(waits_passed, 1)

    def overflow(eng):
        eng.wait_ge(table_ready, 1)
        return eng.value_load(over_i[0:1, 16:17], min_val=0, max_val=MAXOVER)

    block = ctx.enter_context(nc.Block())

    @block.sync
    def _(sp):
        sp.dma_start(ct[:, :], c_table).then_inc(const_in, 16)
        for m in range(MT):
            sp.dma_start(xs[:, m, :], x[m * P:(m + 1) * P, :]).then_inc(x_tile_in[m], 16)
        sp.dma_start(meta_sb[0:META, :], meta).then_inc(x_tile_in[MT], 16)
        sp.dma_start(w_misc, win[:, :, C_IF:C_G]).then_inc(misc_in, 16)
        sp.dma_start(rope, c_rope).then_inc(rope_in, 16)
        sp.wait_ge(pe_kr, 1)

        def load_ml(i, again):
            if again:
                sp.wait_ge(pe_k, i)
            sp.dma_start(wq_s, win[:, :, bass.ds(i * P + C_Q, P)]).then_inc(ml_w[0], 16)
            sp.dma_start(wk_s, win[:, :, bass.ds(i * P + C_K, P)]).then_inc(ml_w[0], 16)
            if again:
                sp.wait_ge(pe_v, i)
            sp.dma_start(wv_s, win[:, :, bass.ds(i * (2 * DV) + C_V, 2 * DV)]).then_inc(ml_w[1], 16)
            if again:
                sp.wait_ge(pe_o, i * 2)
            sp.dma_start(wo_s, win[:, :, bass.ds(i * (2 * DV) + C_O, 2 * DV)]).then_inc(ml_w[2], 16)

        load_ml(0, False)
        with sp.Fori(1, PAIRS) as i:
            load_ml(i, True)
        sp.wait_ge(pe_k, PAIRS)


        def load_at(i, again):
            if again:
                sp.wait_ge(pe_av2, i)
            for k in range(2):
                for c, w0, w in ((0, 0, NOPE), (2 * NOPE, NOPE, ROPE)):
                    sp.dma_start(w_q[:, k, c:c + 2 * w].rearrange("p (h n) -> p h n", h=2),
                                 wuq[:, k, bass.ds(i * 2, 2), w0:w0 + w]).then_inc(at_w, 16)
            sp.dma_start(w_kv, wukv[:, bass.ds(i * (2 * (NOPE + ADV)), 2 * (NOPE + ADV))]).then_inc(at_w, 16)

        load_at(0, False)
        with sp.Fori(1, PAIRS) as i:
            load_at(i, True)
        sp.wait_ge(t_used, H + 1)
        sp.dma_start(w_g[0], win[:, :, C_G:C_G + P]).then_inc(gx_w[0], 16)
        sp.dma_start(w_g[1], wmp[:, :, 0:P]).then_inc(gx_w[1], 16)
        sp.dma_start(w_g[2], win[:, :, C_G + D:C_G + D + P]).then_inc(gx_w[2], 16)
        sp.dma_start(w_g[3], wap[:, :, 0:P]).then_inc(gx_w[3], 16)
        sp.wait_ge(ao_ready, H + 1)
        sp.dma_start(w_o, wop).then_inc(wo_in, 16)
        sp.wait_ge(mix_ready, KT + 1)
        sp.dma_start(gain_f, norm_ffn.partition_broadcast(P)).then_inc(gains_in, 16)
        sp.dma_start(gain_l, norm_final.partition_broadcast(P)).then_inc(gains_in, 16)

        def load_chunk(c, e):
            if c < 8:
                half, part, kh = c // 4, c // 2 % 2, c % 2
                col0 = part * FF + half * BANK
                src = w1v[:, bass.ds(e, 1), 4 * kh:4 * kh + 4, col0:col0 + BANK]
                dst = w1_c[c]
            else:
                src = w2v[:, bass.ds(e, 1), 2 * (c - 8):2 * (c - 8) + 2, :]
                dst = w2_c[c - 8]
            sp.dma_start(dst, src.rearrange("p e k n -> p (e k) n")).then_inc(chunk_in[c], 16)

        def load_b1(e):
            sp.dma_start(b1_row[:, :], b1_dram[:, bass.ds(e, 1), :].rearrange("a e n -> a (e n)")).then_inc(b1_in, 16)

        def load_block(i, e):
            for c in range(SLOTS):
                if c < 8 and c % 2 == 0:
                    sp.wait_ge(half_used, i * 4 + (c // 2 - 3))
                elif c < 8:
                    sp.wait_ge(pe_hid, i * 4 + (c // 2 - 3))
                elif c < SLOTS - 1:
                    sp.wait_ge(down_used, i * 3 + (c - 8 - 2))
                else:
                    sp.wait_ge(pe_y, i)
                load_chunk(c, e)
                if c == 7:
                    load_b1(e)

        for c in range(SLOTS):
            if c == 8:
                sp.wait_ge(b1_stored, 48)
                load_b1(0)
                sp.wait_ge(pe_h, 2 * MT)
            load_chunk(c, 0)
        with sp.Fori(1, E) as i:
            load_block(i, i)
        over = overflow(sp)
        with sp.If(over > 0):
            with sp.Fori(0, over) as n:
                load_block(n + E, sp.value_load(over_i[0:1, bass.ds(n, 1)], min_val=0, max_val=E - 1))
        for m in range(MT):
            sp.wait_ge(out_ready, m + 1)
            sp.dma_start(out[m * P:(m + 1) * P, :], xt[:, m, :]).then_inc(out_stored, 16)
        sp.wait_ge(out_stored, 16 * MT)

    @block.gpsimd
    def _(pool):
        st = Steps(pool, pool_steps)
        with nc.allow_non_contiguous_dma(reason="small vectors turned to columns"):
            pool.dma_start(g_mix, norm_mix.rearrange("(k p) -> p k", p=P)).then_inc(small_in, 16)
            pool.dma_start(g_q, a_norm_q.rearrange("(k p) -> p k", p=P)).then_inc(small_in, 16)
            pool.dma_start(g_kv, a_norm_kv.rearrange("(k p) -> p k", p=P)).then_inc(small_in, 16)
            pool.dma_start(g_m, m_norm.rearrange("h p -> p h")).then_inc(small_in, 16)
            st.alone(nc.gpsimd.memset(gate_bias, 0.0))
            for d in range(2):
                pool.dma_start(gate_bias[32 * d:32 * d + H, :], m_b_i[d].rearrange("(h a) -> h a", a=1)).then_inc(small_in, 16)
                pool.dma_start(gate_bias[64 + 32 * d:64 + 32 * d + H, :], m_b_f[d].rearrange("(h a) -> h a", a=1)).then_inc(small_in, 16)
        st.did(nc.gpsimd.memset(w_if, 0.0))
        pool.wait_ge(const_in, 16)
        for m in range(MT + 1):
            r = P if m < MT else META
            pool.wait_ge(sumsq_x, m + 1)
            st.alone(nc.gpsimd.tensor_scalar(rstd[0:r, m:m + 1], ss[0:r, m:m + 1], 1.0 / D, EPS, ALU.mult, ALU.add))
            nc.gpsimd.tensor_tensor(rstd[0:r, m:m + 1], rstd[0:r, m:m + 1], half_col[0:r, :], ALU.pow).then_inc(rstd_ready, 1)
        pool.wait_ge(misc_in, 16)
        for n in range(4):
            st.did(nc.gpsimd.tensor_copy(w_if[:, :, 32 * n:32 * n + H], w_misc[:, :, H * n:H * (n + 1)]))
        kr0, hr = C_KR - C_IF, ROPE // 2
        for n in range(2):
            st.did(nc.gpsimd.tensor_copy(w_kr[:, 0, :, ROPE * n:ROPE * (n + 1)], w_misc[:, :, kr0:kr0 + ROPE]))
            st.did(nc.gpsimd.tensor_copy(w_kr[:, 1, :, ROPE * n:ROPE * n + hr], w_misc[:, :, kr0 + hr:kr0 + ROPE]))
            st.did(nc.gpsimd.tensor_copy(w_kr[:, 1, :, ROPE * n + hr:ROPE * (n + 1)], w_misc[:, :, kr0:kr0 + hr]))
        st.settle()
        pool.sem_inc(pad_ready, 1)
        nc.gpsimd.memset(zeros, 0.0).then_inc(zeros_ready, 1)
        pool.wait_ge(zeros_ready, 1)
        pool.dma_start(y_dram[E * P:BLOCKS * P, :].rearrange("(p b) n -> p b n", p=P),
                       zeros.unsqueeze(1).broadcast_to([P, BLOCKS - E, D])).then_inc(y_zeroed, 16)
        base = st.end()
        pool.wait_ge(m_stored, 16)
        nc.gpsimd.memset(v_sb[:, :, :, DV:DV + 1], 1.0).then_inc(ones_ready, 1)
        with pool.Fori(0, PAIRS) as i:
            st = Steps(pool, pool_steps, i * 2 + base, 2)
            for hh in range(2):
                for d in range(2):
                    src = m_dram[bass.ds(i * 2 + (32 * d + hh), 1), :]
                    pool.dma_start(m_bc[:, hh, d, :], src.partition_broadcast(P)).then_inc(ml_m, 16)
            for hh in range(2):
                pool.wait_ge(hss_ready, i * 2 + (hh + 1))
                passed(pool)
                st.alone(nc.gpsimd.tensor_scalar(hrs[:, hh, :], hss[:, hh, :], 1.0 / DV, EPS, ALU.mult, ALU.add))
                nc.gpsimd.tensor_tensor(hrs[:, hh, :], hrs[:, hh, :], half_bc, ALU.pow).then_inc(hrs_ready, 1)
            pool.wait_ge(decay_ready, i * 2 + 2)
            st.end()
        base += 2 * PAIRS
        with pool.Fori(0, PAIRS) as i:
            pool.wait_ge(at_w, i * 80 + 80)
            passed(pool)
            hr = ROPE // 2
            for hh in range(2):
                r0 = 2 * NOPE + hh * ROPE
                for n in range(2):
                    last = nc.gpsimd.tensor_copy(w_swap[:, :, hh * ROPE + n * hr:hh * ROPE + (n + 1) * hr],
                                                 w_q[:, :, r0 + (1 - n) * hr:r0 + (2 - n) * hr])
                    last.then_inc(swap_ready, 1)
        base_p = base
        st = Steps(pool, pool_steps, base_p)
        nc.gpsimd.memset(ones3[:, :], 1.0).then_inc(ones_ready, 1)
        pool.dma_start(tok_i, c_tok).then_inc(wr_in, 16)
        pool.dma_start(w_r, w_router.rearrange("(k p) n -> p k n", p=P)).then_inc(wr_in, 16)
        pool.dma_start(b_r, b_router.partition_broadcast(P)).then_inc(wr_in, 16)
        pool.dma_start(disp_dram.rearrange("(p b) a -> p (b a)", p=P), c_zero).then_inc(zero_in, 16)
        pool.wait_ge(ao_ready, H + 1)
        pool.dma_start(b1_f[0:E, :], b1).then_inc(b1f_in, 16)
        pool.wait_ge(b1f_in, 16)
        for n in range(3):
            if n:
                pool.wait_ge(b1_stored, 16 * n)
            st.alone(nc.gpsimd.tensor_copy(b1_part[:, :], b1_f[0:E, :]))
            pool.dma_start(b1_dram[n], b1_part[:, :]).then_inc(b1_stored, 16)
            if n < 2:
                st.alone(nc.gpsimd.tensor_tensor(b1_f[0:E, :], b1_f[0:E, :], b1_part[:, :], ALU.subtract))
        pool.wait_ge(b1_stored, 48)
        pool.dma_start(b2_sb[0:E, :], b2).then_inc(wr_in, 16)
        for m in range(MT):
            pool.wait_ge(xh_ready, m + 1)
            st.alone(nc.gpsimd.tensor_scalar(rstd[:, m:m + 1], ss[:, m:m + 1], 1.0 / D, EPS, ALU.mult, ALU.add))
            nc.gpsimd.tensor_tensor(rstd[:, m:m + 1], rstd[:, m:m + 1], half_col, ALU.pow).then_inc(xh_rstd, 1)
        for m in range(MT):
            pool.wait_ge(xt_ready, m + 1)
            pool.dma_start(xt_dram[m * P:(m + 1) * P, :], xt[:, m, :]).then_inc(xt_stored, 16)
        pool.wait_ge(zero_in, 16)
        for k in range(TOPK):
            pool.wait_ge(rows_ready, k + 1)
            for m in range(MT):
                n = m * TOPK + k
                pool.indirect_dma_start(out=disp_dram, out_offset=bass.IndirectOffsetOnAxis(ap=drow_i[:, n:n + 1], axis=0),
                                        in_=tok_i[:, m:m + 1], in_offset=None).then_inc(placed, 16)
        pool.wait_ge(placed, 16 * MT * TOPK)
        pool.dma_start(disp, disp_dram.rearrange("(p b) a -> p (b a)", p=P)).then_inc(disp_in, 16)
        pool.wait_ge(disp_in, 16)
        pool.wait_ge(xt_stored, 16 * MT)
        pool.wait_ge(pe_h, 2 * MT)

        def gather(i, again=True):
            if again:
                pool.wait_ge(pe_tx, i * 2)
                pool.wait_ge(xg_in, i * 16)
                passed(pool)
            nc.gpsimd.tensor_copy(idx_now, disp[:, bass.ds(i, 1)]).then_inc(idx_ready, 1)
            pool.wait_ge(idx_ready, i + 1)
            passed(pool)
            pool.indirect_dma_start(out=xg, out_offset=None, in_=xt_dram,
                                    in_offset=bass.IndirectOffsetOnAxis(ap=idx_now, axis=0)).then_inc(xg_in, 16)
        over = overflow(pool)
        gather(0, False)
        with pool.Fori(1, E + 1) as i:
            gather(i)
        with pool.If(over > 0):
            with pool.Fori(0, over) as n:
                gather(n + (E + 1))
        pool.wait_ge(y_out, (over + E) * 16)
        pool.wait_ge(pe_y, over + E)
        pool.wait_ge(rows_ready, TOPK + 1)
        passed(pool)
        for m in range(MT):
            for k in range(TOPK):
                n = m * TOPK + k
                pool.indirect_dma_start(out=y_rows[:, n, :], out_offset=None, in_=y_dram,
                                        in_offset=bass.IndirectOffsetOnAxis(ap=yrow_i[:, n:n + 1], axis=0)).then_inc(y_back[m], 16)
        for m in range(MT):
            pool.wait_ge(end_ready, m + 1)
            st.alone(nc.gpsimd.tensor_scalar(rstd[:, m:m + 1], ss[:, m:m + 1], 1.0 / D, EPS, ALU.mult, ALU.add))
            nc.gpsimd.tensor_tensor(rstd[:, m:m + 1], rstd[:, m:m + 1], half_col, ALU.pow).then_inc(end_rstd, 1)

    @block.scalar
    def _(act):
        st = Steps(act, act_steps)
        for m in range(MT + 1):
            r = P if m < MT else META
            src = xs[:, m, :] if m < MT else meta_sb[0:META, :]
            act.wait_ge(x_tile_in[m], 16)
            act.wait_ge(sumsq_x, m)
            nc.scalar.activation(junk[0:r, 0:D], src, ACT.Square, accum_out=ss[0:r, m:m + 1]).then_inc(sumsq_x, 1)
        act.wait_ge(sumsq_x, MT + 1)
        act.wait_ge(minus_abs, 1)
        st.alone(nc.scalar.activation(g_tmp[64:128, :], g_tmp[64:128, :], ACT.Exp))
        nc.scalar.activation(g_tmp[64:128, :], g_tmp[64:128, :], ACT.Ln, bias=ct[64:128, K_ONE:K_ONE + 1]).then_inc(soft_ready, 1)
        act.wait_ge(m_ready, 1)
        nc.scalar.activation(g_tmp[0:64, :], g_tmp[0:64, :], ACT.Exp, scale=-1.0).then_inc(em_rows, 1)
        act.wait_ge(pe_cq, 1)
        for n in range(2):
            nc.scalar.activation(junk[:, n * T:(n + 1) * T], bank(6 + n), ACT.Square).then_inc(sq_ready, 1)
        act.wait_ge(pe_ckv, 1)
        nc.scalar.activation(junk[:, 2 * T:3 * T], bank(0), ACT.Square).then_inc(sq_ready, 1)
        act.wait_ge(if_used, 1)
        nc.scalar.activation(junk[:, 3 * T:3 * T + META], PS[:, 5, 16:32], ACT.Square).then_inc(sq_ready, 1)
        act.wait_ge(pe_sum, 1)
        nc.scalar.activation(root[:, 0:T], bank(3), ACT.Sqrt, scale=1.0 / QL, bias=eps_col).then_inc(root_ready, 1)
        act.wait_ge(pe_sum, 2)
        nc.scalar.activation(root[:, T:2 * T], bank(4), ACT.Sqrt, scale=1.0 / KVL, bias=eps_col).then_inc(root_ready, 1)
        act.wait_ge(pe_sum, 3)
        nc.scalar.activation(root[:, 2 * T:2 * T + META], PS[:, 3, 0:META], ACT.Sqrt, scale=1.0 / KVL, bias=eps_col).then_inc(root_ready, 1)
        act.wait_ge(gates_ready, 1)
        act.dma_start(m_dram[:, :], nm_nat[0:64, META:TK]).then_inc(m_stored, 16)
        base = st.end()
        with act.Fori(0, PAIRS) as i:
            st = Steps(act, act_steps, i * ACT_ML + base, ACT_ML)
            act.wait_ge(ml_m, i * 64 + 64)
            for hh in range(2):
                act.wait_ge(diag_ready, i * 16 + (8 * hh + 8))
                for j in range(MT - 1):
                    st.did(nc.scalar.activation(dec_f(hh, j)[:, (j + 1) * P:T], m_bc[:, hh, 0, (j + 1) * P:T], ACT.Exp, bias=a_pair[:, j, 0, hh:hh + 1]))
                for j in range(1, MT):
                    st.did(nc.scalar.activation(dec_b(hh, j)[:, 0:j * P], m_bc[:, hh, 1, 0:j * P], ACT.Exp, bias=a_pair[:, j, 1, hh:hh + 1]))
                st.did(nc.scalar.activation(dec_f(hh, MT)[0:META, :], m_bc[0:META, hh, 0, :], ACT.Exp, bias=a_pair[0:META, MT, 0, hh:hh + 1]))
                st.did(nc.scalar.activation(diagonal(hh, 0), diagonal(hh, 0), ACT.Exp))
                nc.scalar.activation(diagonal(hh, 1), diagonal(hh, 1), ACT.Exp).then_inc(decay_ready, 1)
                if hh == 0:
                    act.wait_ge(pe_q, i + 1)
                    nc.scalar.mul(qT, bank(0), DQK ** -0.5).then_inc(q_ready, 1)
            for hh in range(2):
                act.wait_ge(pe_o, i * 2 + (hh + 1))
                nc.scalar.activation(o_sb[:, hh, :], bank((7, 0)[hh]), ACT.Exp, scale=-1.0).then_inc(oexp_ready, 1)
                act.wait_ge(pv_used, i * 2 + (hh + 1))
                for m in range(MT):
                    st.alone(nc.scalar.activation(junk2[:, 0:DV], h_sb[:, hh, m, :], ACT.Square, accum_out=hss[:, hh, m:m + 1]))
                act.sem_inc(hss_ready, 1)
            act.wait_ge(t_used, i * 2 + 3)
            st.end()
        base += ACT_ML * PAIRS
        with act.Fori(0, PAIRS) as i:
            act.wait_ge(pe_aq, i * 2 + 1)
            for hh in range(2):
                nc.scalar.copy(qn[:, hh, :], bank(hh)).then_inc(aq_ready, 1)
            act.wait_ge(pe_ak, i + 1)
            for hh in range(2):
                nc.scalar.copy(kn[:, hh, 0:T], bank(4 + hh)).then_inc(ak_ready, 1)
            for n in range(2 * MT + 2):
                if n < 2 * MT:
                    act.wait_ge(max_ready, i * 8 + (n + 1))
                    if n >= 3:
                        act.wait_ge(pe_pt, i * 8 + (n - 2))
                    s2 = PS[:, 2 * (n % 2):2 * (n % 2) + 2, :].rearrange("p a b -> p (a b)")[:, 0:TK]
                    nc.scalar.activation(pr[:, n % 3, :], s2, ACT.Exp, bias=neg_max[:, n:n + 1], scale=(NOPE + ROPE) ** -0.5,
                                         accum_out=row_sum[:, n:n + 1]).then_inc(exp_ready, 1)
                if n > 1:
                    k, m = n - 2, (n - 2) % MT
                    act.wait_ge(pe_pt, i * 8 + (k + 1))
                    if m == 0 and k:
                        act.wait_ge(pe_ao, i * 2 + 1)
                    nc.scalar.copy(prT[:, 0:MT, m * P:(m + 1) * P], bank(4 + k % 2).rearrange("p (a b) -> p a b", a=MT)).then_inc(ptx_ready, 1)
            act.wait_ge(pe_ao, i * 2 + 2)
        def gates(j, more):
            for n in range(4):
                act.wait_ge(pe_g, j * 4 + (n + 1))
                if n % 2 == 0:
                    act.wait_ge(mix_ready, j + 1)
                    nc.scalar.activation(sg[:, n // 2, :], bank(n), ACT.Sigmoid).then_inc(sig_ready, 1)
                if more:
                    src = (win, wmp, win, wap)[n]
                    at = (C_G, 0, C_G + D, 0)[n]
                    act.dma_start(w_g[n], src[:, :, bass.ds(j * P + (at + P), P)]).then_inc(gx_w[n], 16)
        with act.Fori(0, KT - 1) as j:
            gates(j, True)
        gates(KT - 1, False)
        st = Steps(act, act_steps, base)
        for m in range(MT):
            act.wait_ge(h_out, 2 * (m + 1))
            act.wait_ge(xh_ready, m)
            nc.scalar.activation(sq_junk, xs[:, m, :], ACT.Square, accum_out=ss[:, m:m + 1]).then_inc(xh_ready, 1)
        act.wait_ge(xh_ready, MT)
        for m in range(MT):
            for g in range(2):
                act.wait_ge(pe_xt, 2 * m + g + 1)
                nc.scalar.copy(xtT[:, 4 * g:4 * g + 4, m * P:(m + 1) * P], bank(2 * m + g).rearrange("p (a b) -> p a b", a=4)).then_inc(xtT_ready, 1)
        act.wait_ge(ex_in, 1)
        nc.scalar.activation(ex, ex, ACT.Exp).then_inc(ex_ready, 1)
        act.wait_ge(pe_gT, 1)
        nc.scalar.copy(gT[0:E, :], PS[0:E, 2, :]).then_inc(gT_ready, 1)

        def turned_rows(i, g):
            act.wait_ge(pe_tx, i * 2 + (g + 1))
            nc.scalar.copy(xgT[:, 4 * g:4 * g + 4, :], bank(7).rearrange("p (a b) -> p a b", a=4)).then_inc(xgT_ready, 1)

        def turned_act(i, h):
            act.wait_ge(pe_ta, i * 2 + (h + 1))
            nc.scalar.copy(actT[:, 4 * h:4 * h + 4, :], bank(6).rearrange("p (a b) -> p a b", a=4)).then_inc(actT_ready, 1)

        def act_block(i):
            for h in range(2):
                act.wait_ge(g_ready, i * 2 + (h + 1))
                nc.scalar.activation(s_sb, g_sb, ACT.Sigmoid, scale=1.702).then_inc(s_ready, 1)
                if h == 0:
                    turned_act(i, 0)
            turned_rows(i + 1, 0)
            turned_act(i, 1)
            turned_rows(i + 1, 1)
            act.wait_ge(pe_y, i + 1)
            nc.scalar.copy(y_sb, PS[:, 4:6, :].rearrange("p a b -> p (a b)")).then_inc(y_ready, 1)
            act.wait_ge(y_ready, i + 2)
            act.dma_start(y_dram[bass.ds(i * P, P), :], y_sb).then_inc(y_out, 16)
            act.wait_ge(y_out, i * 16 + 16)

        over = overflow(act)
        act.sem_inc(y_ready, 1)
        turned_rows(0, 0)
        turned_rows(0, 1)
        with act.Fori(0, E) as i:
            act_block(i)
        with act.If(over > 0):
            with act.Fori(0, over) as n:
                act_block(n + E)
        for m in range(MT):
            act.wait_ge(h_sum, m + 1)
            act.wait_ge(end_ready, m)
            nc.scalar.activation(sq_junk, xs[:, m, :], ACT.Square, accum_out=ss[:, m:m + 1]).then_inc(end_ready, 1)

    @block.vector
    def _(dve):
        st = Steps(dve, dve_steps)

        def scale(i, hh):
            dve.wait_ge(hrs_ready, i * 2 + (hh + 1))
            r = hrs[:, hh, :].unsqueeze(2).broadcast_to([P, MT, DV])
            nc.vector.tensor_tensor(h_sb[:, hh], h_sb[:, hh], r, ALU.mult).then_inc(h_ready, 1)

        def gated(i, hh):
            dve.wait_ge(pe_t, i * 2 + (hh + 1))
            nc.vector.scalar_tensor_tensor(hmT[:, bass.ds(i * 2 + hh, 1), :], bank(1 + hh).unsqueeze(1), g_pair[:, hh:hh + 1],
                                           o_sb[:, hh:hh + 1, :], ALU.mult, ALU.mult).then_inc(t_used, 1)

        def turned(m, g):
            c, w = (m * P, P) if m < MT else (T, META)
            src = bank(2 * (m % 2) + g)[:, 0:4 * w].rearrange("p (a b) -> p a b", a=4)
            gain = g_mix[:, 4 * g:4 * g + 4].unsqueeze(2).broadcast_to([P, 4, w])
            dve.wait_ge(pe_ut, 2 * m + g + 1)
            nc.vector.tensor_tensor(uT[:, 4 * g:4 * g + 4, c:c + w], src, gain, ALU.mult).then_inc(ut_ready, 1)

        for m in range(MT + 1):
            r = P if m < MT else META
            src = xs[:, m, :] if m < MT else meta_sb[0:META, :]
            dve.wait_ge(rstd_ready, m + 1)
            dve.wait_ge(x_tile_in[m], 16)
            if m >= 2:
                dve.wait_ge(pe_ut, 2 * (m - 1))
            nc.vector.tensor_scalar(un[0:r, m % 2, :], src, rstd[0:r, m:m + 1], None, ALU.mult).then_inc(un_ready, 1)
            if m == 1:
                dve.wait_ge(small_in, 128)
            if m >= 1:
                turned(m - 1, 0)
                turned(m - 1, 1)
        turned(MT, 0)
        turned(MT, 1)
        st.did(nc.vector.memset(li_row[0:64, :], 0.0))
        st.did(nc.vector.memset(lf_row[0:64, :], 0.0))
        st.did(nc.vector.memset(zero_row[0:64, :], 0.0))
        dve.wait_ge(pe_if, 1)
        st.did(nc.vector.tensor_scalar(zif[:, 0:T], bank(4), gate_bias, None, ALU.add))
        nc.vector.tensor_scalar(zif[:, T:TK], PS[:, 5, 0:META], gate_bias, None, ALU.add).then_inc(if_used, 1)
        st.settle()
        dve.wait_ge(if_used, 1)
        nc.vector.scalar_tensor_tensor(g_tmp[64:128, :], zif[64:128, :], -1.0, zif[64:128, :], ALU.mult, ALU.min).then_inc(minus_abs, 1)
        dve.wait_ge(soft_ready, 1)
        st.alone(nc.vector.scalar_tensor_tensor(lf_hi[64:128, :], zif[64:128, :], 0.0, g_tmp[64:128, :], ALU.min, ALU.subtract))
        for row, src, p0 in ((li_row, zif, 0), (lf_row, lf_hi, 64)):
            st.did(nc.vector.tensor_copy(row[0:32, 0:META], src[p0:p0 + 32, T:TK]))
            st.did(nc.vector.tensor_copy(row[0:32, META:TK], src[p0:p0 + 32, 0:T]))
            st.did(nc.vector.tensor_copy(row[32:64, 0:T], src[p0 + 32:p0 + 64, 0:T][:, ::-1]))
        st.settle()
        st.alone(nc.vector.tensor_tensor_scan(b_row[0:64, :], lf_row[0:64, :], zero_row[0:64, :], 0.0, ALU.add, ALU.add))
        st.alone(nc.vector.tensor_tensor(a_row[0:64, :], li_row[0:64, :], b_row[0:64, :], ALU.subtract))
        st.alone(nc.vector.tensor_tensor_scan(top_row[0:64, :], a_row[0:64, :], a_row[0:64, :], 0.0, ALU.max, ALU.max))
        nc.vector.tensor_tensor(g_tmp[0:64, :], b_row[0:64, :], top_row[0:64, :], ALU.add).then_inc(m_ready, 1)
        st.alone(nc.vector.tensor_scalar(top_row[0:64, :], top_row[0:64, :], -1.0, None, ALU.mult))
        dve.wait_ge(em_rows, 1)
        for nat, row in ((a_nat, a_row), (em_nat, g_tmp), (nm_nat, top_row)):
            st.did(nc.vector.tensor_copy(nat[0:32, :], row[0:32, :]))
            st.did(nc.vector.memset(nat[32:64, 0:META], 0.0))
            st.did(nc.vector.tensor_copy(nat[32:64, META:TK], row[32:64, 0:T][:, ::-1]))
        st.settle()
        dve.sem_inc(gates_ready, 1)
        for n in range(3):
            dve.wait_ge(root_ready, n + 1)
            c, w = ((0, T), (T, T), (2 * T, META))[n]
            st.did(nc.vector.reciprocal(root[:, c:c + w], root[:, c:c + w]))
        st.settle()
        for n in range(2):
            st.did(nc.vector.scalar_tensor_tensor(cqT[:, n, :], bank(6 + n), g_q[:, n:n + 1], root[:, 0:T], ALU.mult, ALU.mult))
        st.did(nc.vector.scalar_tensor_tensor(ckvT[:, 0:T], bank(0), g_kv, root[:, T:2 * T], ALU.mult, ALU.mult))
        st.did(nc.vector.scalar_tensor_tensor(ckvT[:, T:TK], PS[:, 5, 16:32], g_kv, root[:, 2 * T:2 * T + META], ALU.mult, ALU.mult))
        dve.wait_ge(pe_kr, 1)
        dve.wait_ge(rope_in, 16)
        st.settle()
        for c, w, a, b in ((0, T, bank(1), bank(2)), (T, META, PS[:, 5, 32:48], PS[:, 5, 48:64])):
            st.did(nc.vector.tensor_tensor(krT[:, c:c + w], a, cos[:, c:c + w], ALU.mult))
            st.alone(nc.vector.tensor_tensor(root[:, 0:w], b, sin[:, c:c + w], ALU.mult))
            st.alone(nc.vector.tensor_tensor(krT[:, c:c + w], krT[:, c:c + w], root[:, 0:w], ALU.add))
        st.settle()
        dve.sem_inc(low_used, 1)
        dve.wait_ge(pe_gt, 1)
        st.did(nc.vector.tensor_copy(a_col[:, 0:MT, :], bank(6)[:, 0:MT * 64].rearrange("p (a b) -> p a b", a=MT)))
        st.did(nc.vector.tensor_copy(a_col[0:META, MT, :], PS[0:META, 6, MT * 64:(MT + 1) * 64]))
        st.did(nc.vector.tensor_copy(em_col, bank(7)[:, 0:MT * 64].rearrange("p (a b) -> p a b", a=MT)))
        st.settle()
        dve.sem_inc(misc_done, 1)
        base = st.end()
        for s in (t_used, ao_ready, mix_ready):
            dve.sem_inc(s, 1)
        a_by = a_col.rearrange("p m (d g) -> p m d g", d=2)
        em_by = em_col.rearrange("p m (d g) -> p m d g", d=2)
        with dve.Fori(0, PAIRS) as i:
            st = Steps(dve, dve_steps, i * DVE_ML + base, DVE_ML)
            st.did(nc.vector.tensor_copy(a_pair[:, 0:MT], a_by[:, 0:MT, :, bass.ds(i * 2, 2)]))
            st.did(nc.vector.tensor_copy(a_pair[0:META, MT], a_by[0:META, MT, :, bass.ds(i * 2, 2)]))
            st.did(nc.vector.tensor_copy(em_pair, em_by[:, :, :, bass.ds(i * 2, 2)]))
            st.did(nc.vector.tensor_copy(g_pair, g_m[:, bass.ds(i * 2, 2)]))
            st.settle()
            dve.wait_ge(ml_m, i * 64 + 64)
            for hh in range(2):
                for d, msk in enumerate((mask_f, mask_b)):
                    for j in range(MT):
                        dst = (dec_f, dec_b)[d](hh, j)[:, j * P:(j + 1) * P]
                        nc.vector.scalar_tensor_tensor(dst, m_bc[:, hh, d, j * P:(j + 1) * P], a_pair[:, j, d, hh:hh + 1], msk,
                                                       ALU.add, ALU.min).then_inc(diag_ready, 1)
            dve.wait_ge(pe_k, i + 1)
            st.did(nc.vector.tensor_copy(kT[:, 0:T], bank(1)))
            nc.vector.tensor_copy(kT[:, T:TK], PS[:, 2, 0:META]).then_inc(k_ready, 1)
            dve.wait_ge(pe_v, i + 1)
            for n in range(2):
                st.did(nc.vector.tensor_copy(v_sb[:, 2 * n:2 * n + 2, :, 0:DV], bank(3 + n).rearrange("p (a b c) -> p a b c", a=2, b=2)))
            nc.vector.tensor_copy(v_sb[0:META, MT, :, 0:DV], PS[0:META, 2, 256:512].rearrange("p (b c) -> p b c", b=2)).then_inc(v_ready, 1)
            for hh in range(2):
                dve.wait_ge(decay_ready, i * 2 + (hh + 1))
                for j in range(MT + 1):
                    n = hh * (MT + 1) + j
                    dve.wait_ge(pe_s, i * 10 + (n + 1))
                    s = bank(5 + n % 2)
                    if j < MT:
                        f, b = dec_f(hh, j)[:, j * P:T], dec_b(hh, j)[:, 0:(j + 1) * P]
                        st.did(nc.vector.tensor_tensor(f, s[:, j * P:T], f, ALU.mult))
                        nc.vector.tensor_tensor(b, s[:, 0:(j + 1) * P], b, ALU.mult).then_inc(s_used, 1)
                    else:
                        f = dec_f(hh, j)[0:META, :]
                        nc.vector.tensor_tensor(f, s[0:META, :], f, ALU.mult).then_inc(s_used, 1)

            def output_gate(hh):
                dve.wait_ge(oexp_ready, i * 2 + (hh + 1))
                st.alone(nc.vector.tensor_scalar(o_sb[:, hh, :], o_sb[:, hh, :], 1.0, None, ALU.add))
                nc.vector.reciprocal(o_sb[:, hh, :], o_sb[:, hh, :]).then_inc(o_used, 1)

            output_gate(0)
            for hh in range(2):
                dve.wait_ge(pe_pv, i * 2 + (hh + 1))
                pv = PS[:, MT * hh:MT * (hh + 1), 0:2 * (DV + 1)].rearrange("p m (d c) -> p m d c", d=2)
                st.did(nc.vector.tensor_copy(rden[:, hh], pv[:, :, :, DV]))
                st.settle()
                st.alone(nc.vector.scalar_tensor_tensor(den[:, hh], rden[:, hh], -1.0, rden[:, hh], ALU.mult, ALU.max))
                st.alone(nc.vector.tensor_tensor(den[:, hh], den[:, hh], em_pair[:, :, :, hh], ALU.max))
                st.alone(nc.vector.reciprocal(rden[:, hh], den[:, hh]))
                for m in range(MT):
                    st.did(nc.vector.tensor_scalar(h_sb[:, hh, m, :], pv[:, m, 0, 0:DV], rden[:, hh, m, 0:1], None, ALU.mult))
                st.settle()
                for m in range(MT):
                    st.did(nc.vector.scalar_tensor_tensor(h_sb[:, hh, m, :], pv[:, m, 1, 0:DV], rden[:, hh, m, 1:2], h_sb[:, hh, m, :], ALU.mult, ALU.add))
                st.settle()
                dve.sem_inc(pv_used, 1)
                scale(i, hh)
            output_gate(1)
            dve.wait_ge(o_used, i * 2 + 2)
            for hh in range(2):
                gated(i, hh)
            dve.wait_ge(t_used, i * 2 + 3)
            st.end()
        base += DVE_ML * PAIRS
        dve.wait_ge(y_zeroed, 16)
        with dve.Fori(0, PAIRS) as i:
            st = Steps(dve, dve_steps, i * DVE_AT + base, DVE_AT)
            dve.wait_ge(pe_aq, i * 2 + 2)
            st.did(nc.vector.tensor_tensor(r_tmp[:, 0, :], bank(2), cos[:, 0:T], ALU.mult))
            st.did(nc.vector.tensor_tensor(r_tmp[:, 1, :], bank(3), sin[:, 0:T], ALU.mult))
            st.settle()
            nc.vector.tensor_tensor(qr, r_tmp[:, 0, :], r_tmp[:, 1, :], ALU.add).then_inc(ar_ready, 1)
            dve.wait_ge(pe_av, i + 1)
            st.did(nc.vector.tensor_copy(kn[:, :, T:TK], PS[:, 6, 0:2 * META].rearrange("p (a b) -> p a b", a=2)))
            st.did(nc.vector.tensor_copy(va[:, 0:2, :], bank(7).rearrange("p (a b) -> p a b", a=2)))
            st.did(nc.vector.tensor_copy(va[0:META, MT, :], PS[0:META, 6, 256:512]))
            dve.wait_ge(pe_av2, i + 1)
            nc.vector.tensor_copy(va[:, 2:4, :], bank(0).rearrange("p (a b) -> p a b", a=2)).then_inc(av_ready, 1)
            for n in range(2 * MT + 4):
                if n < 2 * MT:
                    dve.wait_ge(pe_sc, i * 8 + (n + 1))
                    s2 = PS[:, 2 * (n % 2):2 * (n % 2) + 2, :].rearrange("p a b -> p (a b)")[:, 0:TK]
                    st.alone(nc.vector.reduce_max(neg_max[:, n:n + 1], s2, AX.X))
                    nc.vector.tensor_scalar(neg_max[:, n:n + 1], neg_max[:, n:n + 1], -(NOPE + ROPE) ** -0.5, None, ALU.mult).then_inc(max_ready, 1)
                if 0 < n <= 2 * MT:
                    k = n - 1
                    dve.wait_ge(exp_ready, i * 8 + (k + 1))
                    st.alone(nc.vector.reciprocal(row_inv[:, k:k + 1], row_sum[:, k:k + 1]))
                    nc.vector.tensor_scalar(pr[:, k % 3, :], pr[:, k % 3, :], row_inv[:, k:k + 1], None, ALU.mult).then_inc(p_ready, 1)
                if n in (MT + 1, 2 * MT + 1):
                    dve.wait_ge(pe_pt, i * 8 + (n - 1))
                    nc.vector.tensor_copy(prT[0:META, MT, :], PS[0:META, 6, :]).then_inc(ptm_ready, 1)
                if n in (MT + 3, 2 * MT + 3):
                        hh = (n - MT - 3) // MT
                        dve.wait_ge(pe_ao, i * 2 + (hh + 1))
                        nc.vector.tensor_copy(attT[:, bass.ds(i * 2 + hh, 1), :], bank(7).unsqueeze(1)).then_inc(ao_ready, 1)
            dve.wait_ge(ao_ready, i * 2 + 3)
            st.end()
        base += DVE_AT * PAIRS
        with dve.Fori(0, KT) as j:
            st = Steps(dve, dve_steps, j * DVE_MX + base, DVE_MX)
            dve.wait_ge(sig_ready, j * 2 + 1)
            dve.wait_ge(pe_g, j * 4 + 2)
            st.did(nc.vector.tensor_tensor(mix_tmp, bank(1), sg[:, 0, :], ALU.mult))
            dve.wait_ge(sig_ready, j * 2 + 2)
            dve.wait_ge(pe_g, j * 4 + 4)
            st.alone(nc.vector.tensor_tensor(sg[:, 1, :], bank(3), sg[:, 1, :], ALU.mult))
            nc.vector.tensor_tensor(mixT[:, bass.ds(j, 1), :], mix_tmp.unsqueeze(1), sg[:, 1:2, :], ALU.add).then_inc(mix_ready, 1)
            st.end()
        base += DVE_MX * KT
        st = Steps(dve, dve_steps, base)
        for m in range(MT):
            for c in range(2):
                dve.wait_ge(pe_h, 2 * m + c + 1)
                xo = xs[:, m, c * BANK:(c + 1) * BANK]
                nc.vector.tensor_tensor(xo, xo, bank(2 * m + c), ALU.add).then_inc(h_out, 1)
        dve.wait_ge(gains_in, 32)
        for m in range(MT):
            dve.wait_ge(xh_rstd, m + 1)
            nc.vector.scalar_tensor_tensor(xt[:, m, :], xs[:, m, :], rstd[:, m:m + 1], gain_f, ALU.mult, ALU.mult).then_inc(xt_ready, 1)
        dve.wait_ge(wr_in, 64)
        dve.wait_ge(pe_lg, 1)

        def over_m(v):
            return v.unsqueeze(2).broadcast_to([P, MT, E])

        def over_t(v):
            return v.unsqueeze(1).broadcast_to([P, MT, E])

        V = nc.vector
        st.alone(V.tensor_tensor(lg, bank(0)[:, 0:MT * E].rearrange("p (a b) -> p a b", a=MT), over_t(b_r), ALU.add))
        for m in range(MT):
            st.did(V.max(top8[:, m, :], lg[:, m, :]))
        st.settle()
        V.tensor_tensor(ex, lg, over_m(top8[:, :, 0]), ALU.subtract).then_inc(ex_in, 1)
        st.did(V.tensor_tensor(gt, lg, over_m(top8[:, :, TOPK - 1]), ALU.is_gt))
        st.did(V.tensor_tensor(eq, lg, over_m(top8[:, :, TOPK - 1]), ALU.is_equal))
        st.did(V.memset(tmp_r, 0.0))
        st.settle()
        st.did(V.tensor_reduce(n_gt, gt, AX.X, ALU.add))
        for m in range(MT):
            st.did(V.tensor_tensor_scan(eqn[:, m, :], eq[:, m, :], tmp_r[:, m, :], 0.0, ALU.add, ALU.add))
        st.settle()
        st.alone(V.tensor_tensor(eqn, eqn, over_m(n_gt), ALU.add))
        st.alone(V.scalar_tensor_tensor(eqn, eqn, TOPK + 0.5, eq, ALU.is_lt, ALU.mult))
        V.tensor_tensor(sel, eqn, gt, ALU.add).then_inc(sel_ready, 1)
        dve.wait_ge(sel_ready, 1)
        dve.wait_ge(ex_ready, 1)
        st.alone(V.tensor_tensor(ex, ex, sel, ALU.mult))
        st.alone(V.tensor_reduce(n_gt, ex, AX.X, ALU.add))
        st.alone(V.reciprocal(n_gt, n_gt))
        V.tensor_tensor(ex, ex, over_m(n_gt), ALU.mult).then_inc(g_all_ready, 1)
        for m in range(MT):
            st.did(V.tensor_tensor_scan(rank[:, m, :], sel[:, m, :], tmp_r[:, m, :], 0.0, ALU.add, ALU.add))
        st.settle()
        dve.wait_ge(pe_pos, 1)
        st.did(V.tensor_copy(pos, bank(1)[:, 0:MT * E].rearrange("p (a b) -> p a b", a=MT)))
        st.did(V.tensor_copy(cnt, bank(1)[:, MT * E:(MT + 1) * E]))
        st.settle()
        st.alone(V.tensor_scalar(n_over, cnt, float(P), None, ALU.is_gt))
        st.alone(V.scalar_tensor_tensor(n_over, cnt, 2.0 * P, n_over, ALU.is_gt, ALU.add))
        st.alone(V.scalar_tensor_tensor(n_over, cnt, 3.0 * P, n_over, ALU.is_gt, ALU.add))
        st.alone(V.tensor_tensor_scan(cum_over, n_over, tmp_r[:, 0, :], 0.0, ALU.add, ALU.add))
        st.did(V.tensor_tensor(shift, cum_over, n_over, ALU.subtract))
        st.did(V.tensor_tensor(ov_cmp, cum_over.unsqueeze(1).broadcast_to([P, 16, E]),
                               expert_no[:, 0:16].unsqueeze(2).broadcast_to([P, 16, E]), ALU.is_le))
        st.settle()
        st.did(V.tensor_reduce(ov_f, ov_cmp, AX.X, ALU.add))
        st.alone(V.scalar_tensor_tensor(shift, shift, E - 1.0, expert_no, ALU.add, ALU.subtract))
        st.did(V.tensor_scalar(over_i[:, 0:16], ov_f, E - 1.0, None, ALU.min))
        V.tensor_copy(over_i[:, 16:17], cum_over[:, E - 1:E]).then_inc(table_ready, 1)
        st.did(V.tensor_scalar(jj, pos, P - 0.5, None, ALU.is_gt))
        st.settle()
        st.did(V.tensor_tensor(blk, jj, over_t(shift), ALU.mult))
        st.did(V.scalar_tensor_tensor(selk, pos, 2 * P - 0.5, jj, ALU.is_gt, ALU.add))
        st.settle()
        st.did(V.tensor_tensor(blk, blk, over_t(expert_no), ALU.add))
        st.alone(V.scalar_tensor_tensor(jj, pos, 3 * P - 0.5, selk, ALU.is_gt, ALU.add))
        st.did(V.tensor_tensor(blk, blk, jj, ALU.add))
        st.alone(V.scalar_tensor_tensor(slot_no, jj, -float(P), pos, ALU.mult, ALU.add))
        st.did(V.scalar_tensor_tensor(yrow, blk, float(P), slot_no, ALU.mult, ALU.add))
        st.did(V.scalar_tensor_tensor(drow, slot_no, float(BLOCKS), blk, ALU.mult, ALU.add))
        st.settle()
        for k in range(TOPK):
            st.alone(V.scalar_tensor_tensor(selk, rank, k + 1.0, sel, ALU.is_equal, ALU.mult))
            st.alone(V.tensor_tensor(prod, selk, drow, ALU.mult))
            st.alone(V.tensor_reduce(drow_f[:, :, k], prod, AX.X, ALU.add))
            V.tensor_copy(drow_by[:, :, k], drow_f[:, :, k]).then_inc(rows_ready, 1)
        for k in range(TOPK):
            st.alone(V.scalar_tensor_tensor(selk, rank, k + 1.0, sel, ALU.is_equal, ALU.mult))
            for src, dst in ((yrow, yrow_f), (ex, gate_k)):
                st.alone(V.tensor_tensor(prod, selk, src, ALU.mult))
                st.alone(V.tensor_reduce(dst[:, :, k], prod, AX.X, ALU.add))
        V.tensor_copy(yrow_i, yrow_f.rearrange("p a b -> p (a b)")).then_inc(rows_ready, 1)
        for m in range(MT):
            dve.wait_ge(pe_b2, m + 1)
            V.tensor_tensor(xs[:, m, :], xs[:, m, :], PS[:, 3:5, :].rearrange("p a b -> p (a b)"), ALU.add).then_inc(b2_added, 1)

        def dve_block(i):
            st = Steps(dve, expert_steps, i * 2)
            for h in range(2):
                dve.wait_ge(pe_hid, i * 4 + (2 * h + 1))
                V.tensor_scalar(g_sb, bank(2 * h), 7.0, None, ALU.min).then_inc(g_ready, 1)
                dve.wait_ge(pe_hid, i * 4 + (2 * h + 2))
                V.tensor_scalar(l_sb, bank(2 * h + 1), -7.0, 7.0, ALU.max, ALU.min).then_inc(hid_used, 1)
                dve.wait_ge(hid_used, i * 2 + (h + 1))
                st.alone(V.scalar_tensor_tensor(l_sb, l_sb, 1.0, g_sb, ALU.add, ALU.mult))
                dve.wait_ge(s_ready, i * 2 + (h + 1))
                V.tensor_tensor(act_sb[:, h * BANK:(h + 1) * BANK], l_sb, s_sb, ALU.mult).then_inc(act_ready, 1)
                dve.wait_ge(act_ready, i * 2 + (h + 1))

        over = overflow(dve)
        dve.wait_ge(rows_ready, TOPK + 1)
        with dve.Fori(0, E) as i:
            dve_block(i)
        with dve.If(over > 0):
            with dve.Fori(0, over) as n:
                dve_block(n + E)
        st = Steps(dve, end_steps)
        for m in range(MT + 1):
            if m < MT:
                dve.wait_ge(y_back[m], 16 * TOPK)
                for k in range(TOPK):
                    ins = V.scalar_tensor_tensor(xs[:, m, :], y_rows[:, m * TOPK + k, :], gate_k[:, m, k:k + 1], xs[:, m, :], ALU.mult, ALU.add)
                    if k < TOPK - 1:
                        st.alone(ins)
                ins.then_inc(h_sum, 1)
            if m > 0:
                dve.wait_ge(end_rstd, m)
                V.scalar_tensor_tensor(xt[:, m - 1, :], xs[:, m - 1, :], rstd[:, m - 1:m], gain_l, ALU.mult, ALU.mult).then_inc(out_ready, 1)

    @block.tensor
    def _(pe):
        pe.wait_ge(const_in, 16)
        for m in range(MT + 1):
            r = P if m < MT else META
            pe.wait_ge(un_ready, m + 1)
            for g in range(2):
                if m >= 2:
                    pe.wait_ge(ut_ready, 2 * (m - 2) + g + 1)
                for k in range(4):
                    last = nc.tensor.transpose(bank(2 * (m % 2) + g)[:, k * r:(k + 1) * r], un[0:r, m % 2, (4 * g + k) * P:(4 * g + k + 1) * P], ident[0:r, 0:r])
                last.then_inc(pe_ut, 1)

        def with_u(out, w, c0=0, c1=T):
            return group(pe, out, [(w[:, k], uT[:, k, c0:c1]) for k in range(KT)])

        pe.wait_ge(ut_ready, 2 * (MT + 1))
        pe.wait_ge(pad_ready, 1)
        c0 = C_CKV - C_IF
        with_u(PS[:, 5, 0:16], w_if, T, TK)
        with_u(PS[:, 5, 16:32], w_misc[:, :, c0:c0 + P], T, TK)
        for n in range(2):
            with_u(PS[:, 5, 32 + 16 * n:48 + 16 * n], w_kr[:, n], T, TK)
        with_u(bank(4), w_if).then_inc(pe_if, 1)
        c0 = C_CQ - C_IF
        for n in range(2):
            last = with_u(bank(6 + n), w_misc[:, :, c0 + n * P:c0 + (n + 1) * P])
        last.then_inc(pe_cq, 1)
        c0 = C_CKV - C_IF
        with_u(bank(0), w_misc[:, :, c0:c0 + P]).then_inc(pe_ckv, 1)
        pe.wait_ge(sq_ready, 2)
        group(pe, bank(3), [(ones, junk[:, n * T:(n + 1) * T]) for n in range(2)]).then_inc(pe_sum, 1)
        with_u(bank(1), w_kr[:, 0])
        pe.wait_ge(sq_ready, 4)
        pe.wait_ge(if_used, 1)
        group(pe, bank(4), [(ones, junk[:, 2 * T:3 * T])]).then_inc(pe_sum, 1)
        pe.wait_ge(root_ready, 1)
        group(pe, PS[:, 3, 0:META], [(ones, junk[:, 3 * T:3 * T + META])]).then_inc(pe_sum, 1)
        with_u(bank(2), w_kr[:, 1]).then_inc(pe_kr, 1)
        pe.wait_ge(gates_ready, 1)
        pe.wait_ge(low_used, 1)
        for m in range(MT):
            nc.tensor.transpose(PS[:, 6, m * 64:(m + 1) * 64], a_nat[0:64, META + m * P:META + (m + 1) * P], ident[0:64, 0:64])
            nc.tensor.transpose(PS[:, 7, m * 64:(m + 1) * 64], em_nat[0:64, META + m * P:META + (m + 1) * P], ident[0:64, 0:64])
        nc.tensor.transpose(PS[0:META, 6, MT * 64:(MT + 1) * 64], a_nat[0:64, 0:META], ident[0:64, 0:64]).then_inc(pe_gt, 1)
        pe.wait_ge(misc_done, 1)
        pe.wait_ge(ones_ready, 1)
        with pe.Fori(0, PAIRS) as i:
            pe.wait_ge(ml_w[0], i * 32 + 32)
            with_u(bank(0), wq_s).then_inc(pe_q, 1)
            pe.wait_ge(t_used, i * 2 + 1)
            with_u(bank(1), wk_s)
            with_u(PS[:, 2, 0:META], wk_s, T, TK).then_inc(pe_k, 1)
            pe.wait_ge(ml_w[1], i * 16 + 16)
            for m in range(MT):
                group(pe, PS[:, 3 + m // 2, (m % 2) * 256:(m % 2 + 1) * 256], [(uT[:, k, m * P:(m + 1) * P], wv_s[:, k, :]) for k in range(KT)])
            pe.wait_ge(k_ready, i + 1)
            group(pe, PS[0:META, 2, 256:512], [(uT[:, k, T:TK], wv_s[:, k, :]) for k in range(KT)]).then_inc(pe_v, 1)
            pe.wait_ge(q_ready, i + 1)
            for hh in range(2):
                for j in range(MT + 1):
                    n = hh * (MT + 1) + j
                    if n >= 2:
                        pe.wait_ge(s_used, i * 10 + (n - 1))
                    r = P if j < MT else META
                    h0 = DQK * hh
                    if j == MT:
                        passed(pe)
                    nc.tensor.matmul(PS[0:r, 5 + n % 2, :], kT[h0:h0 + DQK, j * P:j * P + r], qT[h0:h0 + DQK, :], start=True, stop=True).then_inc(pe_s, 1)
            pe.wait_ge(ml_w[2], i * 16 + 16)
            with_u(bank(7), wo_s[:, :, 0:DV]).then_inc(pe_o, 1)
            pe.wait_ge(v_ready, i + 1)
            for hh in range(2):
                if hh == 1:
                    pe.wait_ge(oexp_ready, i * 2 + 1)
                pe.wait_ge(s_used, i * 10 + 5 * (hh + 1))
                for m in range(MT):
                    c = slice(m * P, (m + 1) * P)
                    fwd = [(dec_f(hh, j)[:, c], v_sb[:, j, hh, :]) for j in range(m + 1)] + [(dec_f(hh, MT)[0:META, c], v_sb[0:META, MT, hh, :])]
                    bwd = [(dec_b(hh, j)[:, c], v_sb[:, j, hh, :]) for j in range(m, MT)]
                    group(pe, PS[:, MT * hh + m, 0:DV + 1], fwd)
                    last = group(pe, PS[:, MT * hh + m, DV + 1:2 * (DV + 1)], bwd)
                last.then_inc(pe_pv, 1)
            pe.wait_ge(pv_used, i * 2 + 1)
            with_u(bank(0), wo_s[:, :, DV:2 * DV]).then_inc(pe_o, 1)
            for hh in range(2):
                if hh == 1:
                    pe.wait_ge(oexp_ready, i * 2 + 2)
                pe.wait_ge(h_ready, i * 2 + (hh + 1))
                for m in range(MT):
                    last = nc.tensor.transpose(PS[:, 1 + hh, m * P:(m + 1) * P], h_sb[:, hh, m, :], ident)
                last.then_inc(pe_t, 1)
        pe.wait_ge(t_used, H + 1)
        with pe.Fori(0, PAIRS) as i:
            pe.wait_ge(swap_ready, i * 4 + 4)
            pe.wait_ge(ao_ready, i * 2 + 1)
            for hh in range(2):
                last = group(pe, bank(hh), [(w_q[:, k, hh * NOPE:(hh + 1) * NOPE], cqT[:, k, :]) for k in range(2)])
            last.then_inc(pe_aq, 1)
            group(pe, bank(2), [(w_q[:, k, 2 * NOPE:2 * (NOPE + ROPE)], cqT[:, k, :]) for k in range(2)])
            group(pe, bank(3), [(w_swap[:, k], cqT[:, k, :]) for k in range(2)]).then_inc(pe_aq, 1)
            for hh in range(2):
                wk = w_kv[:, hh * (NOPE + ADV):hh * (NOPE + ADV) + NOPE]
                group(pe, bank(4 + hh), [(wk, ckvT[:, 0:T])])
                last = group(pe, PS[:, 6, hh * META:(hh + 1) * META], [(wk, ckvT[:, T:TK])])
            last.then_inc(pe_ak, 1)
            wv = w_kv.rearrange("p (h c) -> p h c", h=2)[:, :, NOPE:NOPE + ADV]
            for m in range(2):
                group(pe, PS[:, 7, m * 256:(m + 1) * 256], [(ckvT[:, m * P:(m + 1) * P], wv)])
            group(pe, PS[0:META, 6, 256:512], [(ckvT[:, T:TK], wv)]).then_inc(pe_av, 1)
            pe.wait_ge(aq_ready, i * 2 + 2)
            for m in range(2, 4):
                last = group(pe, PS[:, 0, (m - 2) * 256:(m - 1) * 256], [(ckvT[:, m * P:(m + 1) * P], wv)])
            last.then_inc(pe_av2, 1)
            pe.wait_ge(ar_ready, i + 1)
            pe.wait_ge(ak_ready, i * 2 + 2)
            pe.wait_ge(av_ready, i + 1)
            for n in range(2 * MT + 3):
                if n < 2 * MT:
                    hh, m = n // MT, n % MT
                    if n >= 2:
                        pe.wait_ge(exp_ready, i * 8 + (n - 1))
                    h0 = ROPE * hh
                    for b, c, w in ((2 * (n % 2), 0, T), (2 * (n % 2) + 1, T, META)):
                        last = group(pe, PS[:, b, 0:w], [(qn[:, hh, m * P:(m + 1) * P], kn[:, hh, c:c + w]),
                                                         (qr[h0:h0 + ROPE, m * P:(m + 1) * P], krT[h0:h0 + ROPE, c:c + w])])
                    last.then_inc(pe_sc, 1)
                if n in (MT + 2, 2 * MT + 2):
                    hh = (n - MT - 2) // MT
                    pe.wait_ge(ptx_ready, i * 8 + (hh + 1) * MT)
                    pe.wait_ge(ptm_ready, i * 2 + (hh + 1))
                    if hh == 1:
                        pe.wait_ge(ao_ready, i * 2 + 2)
                    vs = [(va[:, j, hh * ADV:(hh + 1) * ADV], prT[:, j, :]) for j in range(MT)]
                    vs.append((va[0:META, MT, hh * ADV:(hh + 1) * ADV], prT[0:META, MT, :]))
                    group(pe, bank(7), vs).then_inc(pe_ao, 1)
                if 1 < n < 2 * MT + 2:
                    k, hh, m = n - 2, (n - 2) // MT, (n - 2) % MT
                    pe.wait_ge(p_ready, i * 8 + (k + 1))
                    if k >= 2:
                        pe.wait_ge(ptx_ready, i * 8 + (k - 1))
                    if m == 0 and hh:
                        pe.wait_ge(ptm_ready, i * 2 + 1)
                    for j in range(MT):
                        nc.tensor.transpose(PS[:, 4 + k % 2, j * P:(j + 1) * P], pr[:, k % 3, j * P:(j + 1) * P], ident)
                    nc.tensor.transpose(PS[0:META, 6, m * P:(m + 1) * P], pr[:, k % 3, T:TK], ident).then_inc(pe_pt, 1)
        pe.wait_ge(ao_ready, H + 1)
        with pe.Fori(0, KT) as j:
            for n in range(4):
                pe.wait_ge(gx_w[n], j * 16 + 16)
                if n == 1:
                    pe.wait_ge(mix_ready, j + 1)
                if n == 3:
                    pe.wait_ge(sig_ready, j * 2 + 1)
                src = (uT[:, :, 0:T], hmT, uT[:, :, 0:T], attT)[n]
                group(pe, bank(n), [(w_g[n][:, k], src[:, k, :]) for k in range(KT)]).then_inc(pe_g, 1)
        pe.wait_ge(mix_ready, KT + 1)
        pe.wait_ge(wo_in, 16)
        for m in range(MT):
            for c in range(2):
                group(pe, bank(2 * m + c), [(mixT[:, k, m * P:(m + 1) * P], w_o[:, k, c * BANK:(c + 1) * BANK]) for k in range(KT)]).then_inc(pe_h, 1)
        for m in range(MT):
            pe.wait_ge(xt_ready, m + 1)
            pe.wait_ge(h_out, 2 * MT)
            pe.wait_ge(xh_ready, MT)
            for g in range(2):
                for k in range(4):
                    last = nc.tensor.transpose(PS[:, 2 * m + g, k * P:(k + 1) * P], xt[:, m, (4 * g + k) * P:(4 * g + k + 1) * P], ident)
                last.then_inc(pe_xt, 1)
        pe.wait_ge(wr_in, 64)
        pe.wait_ge(xtT_ready, 2 * MT)
        for m in range(MT):
            last = group(pe, PS[:, 0, m * E:(m + 1) * E], [(xtT[:, k, m * P:(m + 1) * P], w_r[:, k, :]) for k in range(KT)])
        last.then_inc(pe_lg, 1)
        pe.wait_ge(sel_ready, 1)
        for m in range(MT):
            group(pe, PS[:, 1, m * E:(m + 1) * E], [(ones, sel[:, n, :]) for n in range(m)] + [(before, sel[:, m, :])])
        group(pe, PS[:, 1, MT * E:(MT + 1) * E], [(ones, sel[:, n, :]) for n in range(MT)]).then_inc(pe_pos, 1)
        pe.wait_ge(g_all_ready, 1)
        for m in range(MT):
            last = nc.tensor.transpose(PS[0:E, 2, m * P:(m + 1) * P], ex[:, m, :], ident)
        last.then_inc(pe_gT, 1)
        pe.wait_ge(gT_ready, 1)
        for m in range(MT):
            pe.wait_ge(b2_added, m)
            for c in range(2):
                last = nc.tensor.matmul(bank(3 + c), gT[0:E, m * P:(m + 1) * P], b2_sb[0:E, c * BANK:(c + 1) * BANK], start=True, stop=True)
            last.then_inc(pe_b2, 1)
        pe.wait_ge(b2_added, MT)

        def turn_rows(i, g):
            pe.wait_ge(xg_in, i * 16 + 16)
            pe.wait_ge(xgT_ready, i * 2 + g)
            for k in range(4):
                last = nc.tensor.transpose(PS[:, 7, k * P:(k + 1) * P], xg[:, (4 * g + k) * P:(4 * g + k + 1) * P], ident)
            last.then_inc(pe_tx, 1)

        def turn_act(i, h):
            pe.wait_ge(act_ready, i * 2 + (h + 1))
            for k in range(4):
                last = nc.tensor.transpose(PS[:, 6, k * P:(k + 1) * P], act_sb[:, (4 * h + k) * P:(4 * h + k + 1) * P], ident)
            last.then_inc(pe_ta, 1)

        def down(i, h):
            pe.wait_ge(actT_ready, i * 2 + (h + 1))
            for k in range(4 * h, 4 * h + 4):
                if k % 2 == 0:
                    pe.wait_ge(chunk_in[8 + k // 2], i * 16 + 16)
                for c in range(2):
                    last = nc.tensor.matmul(bank(4 + c), actT[:, k, :], w2_c[k // 2][:, k % 2, c * BANK:(c + 1) * BANK], start=k == 0, stop=k == KT - 1)
                if k == KT - 1:
                    last.then_inc(pe_y, 1)
                elif k % 2 == 1:
                    last.then_inc(down_used, 1)

        def pe_block(i):
            pe.wait_ge(xgT_ready, i * 2 + 2)
            pe.wait_ge(b1_in, i * 16 + 16)
            pe.wait_ge(ones_ready, 2)
            for h in range(2):
                for part in range(2):
                    b = 2 * h + part
                    col0 = part * FF + h * BANK
                    nc.tensor.matmul(bank(b), ones3[:, :], b1_row[:, col0:col0 + BANK], start=True, stop=False)
                    for k in range(KT):
                        c = 2 * b + k // 4
                        if k % 4 == 0:
                            pe.wait_ge(chunk_in[c], i * 16 + 16)
                        if b == 3 and k == 4:
                            turn_act(i, 0)
                        last = nc.tensor.matmul(bank(b), xgT[:, k, :], w1_c[c][:, k % 4, :], start=False, stop=k == KT - 1)
                        if k == 3:
                            last.then_inc(half_used, 1)
                    last.then_inc(pe_hid, 1)
            turn_rows(i + 1, 0)
            pe.wait_ge(y_ready, i + 1)
            down(i, 0)
            turn_act(i, 1)
            turn_rows(i + 1, 1)
            down(i, 1)

        over = overflow(pe)
        turn_rows(0, 0)
        turn_rows(0, 1)
        with pe.Fori(0, E) as i:
            pe_block(i)
        with pe.If(over > 0):
            with pe.Fori(0, over) as n:
                pe_block(n + E)


_CORE = ["norm_mix", "w_in", "m_b_i", "m_b_f", "m_norm", "w_m_proj", "a_w_uq", "a_w_ukv", "a_norm_q",
         "a_norm_kv", "w_a_proj", "w_out", "norm_ffn", "w_router", "b_router", "w1", "b1", "w2", "b2"]


def kernel(**inputs):
    import concourse.bacc as bacc
    from concourse.bass_utils import run_bass_kernel_spmd

    nc = bacc.Bacc("TRN2", target_bir_lowering=False, num_devices=1)
    arrays = {"x": np.ascontiguousarray(inputs["x"])[0], "meta_tokens": np.ascontiguousarray(inputs["meta_tokens"])}
    for name in _CORE:
        arrays[name] = np.ascontiguousarray(inputs[name])[0]
    arrays["norm_final"] = np.ascontiguousarray(inputs["norm_final"])
    arrays.update(constant_tables())
    args = [nc.dram_tensor(f"in_{n}", a.shape, mybir.dt.from_np(a.dtype), kind="ExternalInput").ap() for n, a in arrays.items()]
    out = nc.dram_tensor("out_dram", (T, D), F32, kind="ExternalOutput").ap()
    program(nc, *args, out)
    r = run_bass_kernel_spmd(nc, [{f"in_{n}": a for n, a in arrays.items()}], core_ids=[0])
    return r.results[0]["out_dram"].reshape(1, T, D)
```
